# Optimizing a Trainium2 kernel written in Bass

```python
import jax, jax.numpy as jnp
from jax import lax
import numpy as np

D_MODEL = 2048
BATCH = 1
SEQ = 256
DEPTH = 2

PLE_DIM = 256
N_MIXERS = 2
RET_HEADS = 8
RET_QK_DIM = D_MODEL // RET_HEADS
RET_V_DIM = 2 * D_MODEL // RET_HEADS
RET_PROJ = 2 * RET_HEADS * RET_QK_DIM + 2 * RET_HEADS * RET_V_DIM
RET_CHUNK = 128
ROPE_BASE = 10000.0
POOL_WIDTH = 2 * D_MODEL
POOL_WINDOWS = (2, 4, 8, 16)
POOL_GROUPS = len(POOL_WINDOWS)
POOL_GROUP_DIM = POOL_WIDTH // POOL_GROUPS
N_RET_LAYERS = (DEPTH + 1) // 2
N_POOL_LAYERS = DEPTH // 2
NORM_EPS = 1e-6
GN_EPS = 1e-5

kernel_name = "retnet_pool_interleaved_hybrid"

def rms_norm(x, gain):
    x32 = x.astype(jnp.float32)
    y = x32 * lax.rsqrt(jnp.mean(x32 * x32, axis=-1, keepdims=True) + NORM_EPS)
    return (y * gain.astype(jnp.float32)).astype(x.dtype)

def rotate_pairs(x, cos, sin):
    xr = x.reshape(x.shape[:-1] + (x.shape[-1] // 2, 2))
    x0, x1 = xr[..., 0], xr[..., 1]
    out = jnp.stack([x0 * cos - x1 * sin, x1 * cos + x0 * sin], axis=-1)
    return out.reshape(x.shape)

def retention_branch(xn, w_in, w_out):
    b, s, _ = xn.shape
    h, dk, dv, c = RET_HEADS, RET_QK_DIM, RET_V_DIM, RET_CHUNK
    n = s // c
    f32 = jnp.float32
    q, k, v, g = jnp.split(xn @ w_in, [h * dk, 2 * h * dk, 2 * h * dk + h * dv], axis=-1)
    q = q.reshape(b, s, h, dk).astype(f32)
    k = k.reshape(b, s, h, dk).astype(f32)
    v = v.reshape(b, s, h, dv).astype(f32)
    pos = jnp.arange(s, dtype=f32)
    freq = ROPE_BASE ** (-jnp.linspace(0.0, 1.0, dk // 2, dtype=f32))
    ang = pos[:, None] * freq[None, :]
    cos = jnp.cos(ang)[None, :, None, :]
    sin = jnp.sin(ang)[None, :, None, :]
    q = rotate_pairs(q, cos, sin)
    k = rotate_pairs(k, cos, sin) * (dk ** -0.5)
    log_gamma = jnp.log1p(-(2.0 ** (-5.0 - jnp.arange(h, dtype=f32))))
    idx = jnp.arange(c, dtype=f32)
    diff = idx[:, None] - idx[None, :]
    inner_decay = jnp.where(diff[None] >= 0,
                            jnp.exp(jnp.maximum(diff, 0.0)[None] * log_gamma[:, None, None]),
                            0.0)
    q_decay = jnp.exp((idx + 1.0)[:, None] * log_gamma[None, :])
    k_decay = jnp.exp((c - 1.0 - idx)[:, None] * log_gamma[None, :])
    chunk_decay = jnp.exp(c * log_gamma)
    qc = q.reshape(b, n, c, h, dk)
    kc = k.reshape(b, n, c, h, dk)
    vc = v.reshape(b, n, c, h, dv)
    scores = jnp.einsum('bnihd,bnjhd->bnhij', qc, kc) * inner_decay
    y_inner = jnp.einsum('bnhij,bnjhv->bnihv', scores, vc)

    def step(state, inp):
        q_n, k_n, v_n = inp
        y = jnp.einsum('bihd,bhdv->bihv', q_n, state) * q_decay[None, :, :, None]
        state = state * chunk_decay[None, :, None, None] + jnp.einsum(
            'bjhd,bjhv->bhdv', k_n * k_decay[None, :, :, None], v_n)
        return state, y

    state0 = jnp.zeros((b, h, dk, dv), f32)
    _, y_cross = lax.scan(step, state0, (jnp.moveaxis(qc, 1, 0), jnp.moveaxis(kc, 1, 0),
                                         jnp.moveaxis(vc, 1, 0)))
    y = (y_inner + jnp.moveaxis(y_cross, 0, 1)).reshape(b, s, h, dv)
    mu = jnp.mean(y, axis=-1, keepdims=True)
    var = jnp.mean(jnp.square(y - mu), axis=-1, keepdims=True)
    y = ((y - mu) * lax.rsqrt(var + GN_EPS)).reshape(b, s, h * dv).astype(xn.dtype)
    return (jax.nn.silu(g) * y) @ w_out

def pool_branch(xn, w_in, w_group, scale, w_out):
    b, s, _ = xn.shape
    u, g = jnp.split(xn @ w_in, 2, axis=-1)
    u32 = u.astype(jnp.float32)
    csum = jnp.cumsum(u32, axis=1)
    t = jnp.arange(s)
    outs = []
    for gi, w in enumerate(POOL_WINDOWS):
        lo, hi = gi * POOL_GROUP_DIM, (gi + 1) * POOL_GROUP_DIM
        c_g = csum[..., lo:hi]
        c_lag = jnp.pad(c_g, ((0, 0), (w, 0), (0, 0)))[:, :s]
        cnt = jnp.minimum(t + 1, w).astype(jnp.float32)[None, :, None]
        outs.append((c_g - c_lag) / cnt - u32[..., lo:hi])
    d = jnp.stack(outs, axis=2).astype(xn.dtype)
    mixed = jnp.einsum('bsgc,gce->bsge', d, w_group).reshape(b, s, POOL_WIDTH) * scale
    return (mixed * jax.nn.silu(g)) @ w_out

def setup_inputs(seed: int = 0) -> dict:
    key = jax.random.key(seed)
    ks = jax.random.split(key, 16)
    nrm = jax.random.normal
    f32 = jnp.float32
    x = nrm(ks[0], (BATCH, SEQ, D_MODEL), f32)
    p = nrm(ks[1], (DEPTH, BATCH, SEQ, PLE_DIM), f32)
    ret_norm = 1.0 + 0.02 * nrm(ks[2], (N_RET_LAYERS, D_MODEL), f32)
    ret_w_in = nrm(ks[3], (N_RET_LAYERS, D_MODEL, RET_PROJ), f32) * D_MODEL ** -0.5
    ret_w_out = nrm(ks[4], (N_RET_LAYERS, RET_HEADS * RET_V_DIM, D_MODEL), f32) * (RET_HEADS * RET_V_DIM) ** -0.5
    pool_norm = 1.0 + 0.02 * nrm(ks[5], (N_POOL_LAYERS, D_MODEL), f32)
    pool_w_in = nrm(ks[6], (N_POOL_LAYERS, D_MODEL, 2 * POOL_WIDTH), f32) * D_MODEL ** -0.5
    pool_w_group = nrm(ks[7], (N_POOL_LAYERS, POOL_GROUPS, POOL_GROUP_DIM, POOL_GROUP_DIM), f32) * POOL_GROUP_DIM ** -0.5
    pool_scale = 1.0 + 0.1 * nrm(ks[8], (N_POOL_LAYERS, POOL_WIDTH), f32)
    pool_w_out = nrm(ks[9], (N_POOL_LAYERS, POOL_WIDTH, D_MODEL), f32) * POOL_WIDTH ** -0.5
    ple_norm = 1.0 + 0.02 * nrm(ks[10], (DEPTH, D_MODEL), f32)
    ple_w_gate = nrm(ks[11], (DEPTH, D_MODEL, D_MODEL), f32) * D_MODEL ** -0.5
    ple_w_proj = nrm(ks[12], (DEPTH, PLE_DIM, D_MODEL), f32) * PLE_DIM ** -0.5
    final_norm = 1.0 + 0.02 * nrm(ks[13], (D_MODEL,), f32)
    return {"x": x, "p": p, "ret_norm": ret_norm, "ret_w_in": ret_w_in, "ret_w_out": ret_w_out,
            "pool_norm": pool_norm, "pool_w_in": pool_w_in, "pool_w_group": pool_w_group,
            "pool_scale": pool_scale, "pool_w_out": pool_w_out, "ple_norm": ple_norm,
            "ple_w_gate": ple_w_gate, "ple_w_proj": ple_w_proj, "final_norm": final_norm}

def reference(x, p, ret_norm, ret_w_in, ret_w_out, pool_norm, pool_w_in, pool_w_group,
              pool_scale, pool_w_out, ple_norm, ple_w_gate, ple_w_proj, final_norm):
    h = x
    for i in range(DEPTH):
        j = i // N_MIXERS
        if i % N_MIXERS == 0:
            h = h + retention_branch(rms_norm(h, ret_norm[j]), ret_w_in[j], ret_w_out[j])
        else:
            h = h + pool_branch(rms_norm(h, pool_norm[j]), pool_w_in[j], pool_w_group[j],
                                pool_scale[j], pool_w_out[j])
        gate = jax.nn.sigmoid(rms_norm(h, ple_norm[i]) @ ple_w_gate[i])
        h = h + gate * (p[i] @ ple_w_proj[i])
    return rms_norm(h, final_norm)


_drawn_inputs = setup_inputs


def setup_inputs(seed=0):
    import zlib

    import numpy as np

    out = dict(_drawn_inputs(seed))
    spreads = {}
    factors = {'ret_norm': 2.847, 'pool_norm': 5.36, 'ple_norm': 50.847, 'final_norm': 7.686}
    for name, (base, spread) in spreads.items():
        noise = np.random.default_rng([zlib.crc32(name.encode()), seed]).standard_normal(out[name].shape)
        drawn = base * np.exp(spread * noise) if base else spread * noise
        out[name] = __import__('jax').numpy.asarray(drawn.astype(out[name].dtype))
    for name, factor in factors.items():
        out[name] = (out[name] * factor).astype(out[name].dtype)
    return out
```

```python
from contextlib import ExitStack

import concourse.bass as bass
from concourse import mybir

F32 = mybir.dt.float32
F32R = mybir.dt.float32r
I32 = mybir.dt.int32
ALU = mybir.AluOpType
ACT = mybir.ActivationFunctionType
AX = mybir.AxisListType

P = 128
D = 2048
TT = 2
SEQ = TT * P
COL = 512
NC = D // COL
KD = D // P
HEADS = 8
DK = D // HEADS
WINDOWS = (2, 4, 8, 16)
GROUPS = len(WINDOWS)
GDIM = 2 * D // GROUPS
KG = GDIM // P
KP = 2
NORM_EPS = 1e-6
GN_EPS = 1e-5

UNIT = 2
PIECE = 4
RING = 4
RAW = 4
KD_U = KD // UNIT
RO_U = COL // P // UNIT
PO_U = KG // UNIT

HEAD_U = 3 * KD_U + NC * RO_U
GROUP_U = 4 * KD_U + 2 * PO_U + NC * PO_U
EMB_U = NC
GATE_U = NC * KD_U
RET0 = 0
RET1 = 3 * KD_U
CLOSE_A = RET1 + (HEADS - 1) * HEAD_U
POOL0 = CLOSE_A + EMB_U + NC * RO_U + GATE_U
POOL1 = POOL0 + 4 * KD_U + 2 * PO_U
CLOSE_B = POOL1 + (GROUPS - 1) * GROUP_U
UNITS = CLOSE_B + EMB_U + NC * PO_U + GATE_U
PIECES = UNITS * UNIT // PIECE
STAGES = 5
ACT_OUT = 2
MAGIC = 0x5F3759DF
NEWTON = 3
RS_STEPS = 3 + 3 * NEWTON
HEAD_STEPS = 3 + RS_STEPS
O_RET = (HEADS - 2) * NC


class Steps:

    def __init__(self, eng, sem):
        self.eng, self.sem, self.n, self.base = eng, sem, 0, 0

    def mark(self, ins):
        ins.then_inc(self.sem, 1)
        self.n += 1

    def wait(self):
        self.eng.wait_ge(self.sem, self.base + self.n)


def trunk(nc, stream, x, pT, gains, pool_scale, final_gain, rope, decay, band, counts, ident, out):
    with ExitStack() as ctx:
        def sb(name, shape, dt):
            return ctx.enter_context(nc.sbuf_tensor(name, shape, dt))

        def sem(name):
            return ctx.enter_context(nc.semaphore(name))

        w_raw = sb("w_raw", [P, RAW, PIECE * COL], F32)
        w_hi = sb("w_hi", [P, RING, UNIT * COL], F32R)
        w_lo = sb("w_lo", [P, RING, UNIT * COL], F32R)
        xa_hi = sb("xa_hi", [P, KD, SEQ], F32R)
        xa_lo = sb("xa_lo", [P, KD, SEQ], F32R)
        oT_hi = sb("oT_hi", [P, KG, SEQ], F32R)
        oT_lo = sb("oT_lo", [P, KG, SEQ], F32R)
        h = sb("h", [P, TT, D], F32)
        emb = sb("emb", [P, TT, D], F32)
        pT_hi = sb("pT_hi", [P, 2, KP, SEQ], F32R)
        pT_lo = sb("pT_lo", [P, 2, KP, SEQ], F32R)
        sig = sb("sig", [P, TT, COL], F32)
        p_raw = sig[:].rearrange("p t (k n) -> p t k n", n=SEQ)
        idn = sb("idn", [P, P], F32)
        gain = sb("gain", [P, STAGES - 1, KD], F32)
        pscale = sb("pscale", [P, GROUPS * KG], F32)
        ssq = sb("ssq", [P, STAGES, TT, NC], F32)
        rs = sb("rs", [P, STAGES, TT], F32)
        stats = sb("stats", [P, TT, 6], F32)
        mv = sb("mv", [P, TT, 2], F32)
        rstd = sb("rstd", [P, TT], F32)
        nx2 = sb("nx2", [P, TT], F32)
        nt2 = sb("nt2", [P, TT], F32)
        ni2 = sb("ni2", [P, TT], I32)
        junk = sb("junk", [P, TT, COL], mybir.dt.bfloat16)

        ARENA_KB = 48
        arena0 = nc.sbuf_base
        sb("arena", [P, ARENA_KB * 256], F32)
        warm = sb("warm", [P, 1], F32)

        def at(name, kb, shape, dt):
            return nc.alloc_sbuf_tensor_at(name, shape, dt, offset=arena0 + kb * 1024)

        ropec = at("ropec", 0, [P, TT, COL], F32)
        ropes = at("ropes", 4, [P, TT, COL], F32)
        dec = at("dec", 8, [P, HEADS, SEQ], F32)
        qk = at("qk", 16, [P, TT, COL], F32)
        qk2 = at("qk2", 20, [P, TT, COL], F32)
        pr = at("pr", 20, [P, SEQ + P], F32)
        pr_hi = at("pr_hi", 22, [P, SEQ + P], F32R)
        qkT_hi = at("qkT_hi", 24, [P, 4, SEQ], F32R)
        qkT_lo = at("qkT_lo", 28, [P, 4, SEQ], F32R)
        v_hi = at("v_hi", 32, [P, TT, COL], F32R)
        v_lo = at("v_lo", 36, [P, TT, COL], F32R)
        yn = at("yn", 40, [P, TT, COL], F32)
        pr_lo = at("pr_lo", 44, [P, SEQ + P], F32R)
        xb_hi = at("xb_hi", 0, [P, KD, SEQ], F32R)
        xb_lo = at("xb_lo", 16, [P, KD, SEQ], F32R)
        u_hi = at("u_hi", 0, [P, TT, COL], F32R)
        u_lo = at("u_lo", 4, [P, TT, COL], F32R)
        dT_hi = at("dT_hi", 8, [P, KG, SEQ], F32R)
        dT_lo = at("dT_lo", 16, [P, KG, SEQ], F32R)
        gm = at("gm", 24, [P, 2, TT, COL], F32)
        bnd = at("bnd", 32, [P, GROUPS, SEQ + P], F32R)
        bnd_raw = at("bnd_raw", 38, [P, GROUPS, SEQ + P], F32)
        d_tmp = at("d_tmp", 38, [P, 4, SEQ], F32)
        inv = at("inv", 44, [P, GROUPS, SEQ], F32)
        fgain = at("fgain", 32, [P, D], F32)

        acc = {n: [ctx.enter_context(nc.psum_tensor(f"acc{n}{t}", [P, COL], F32)) for t in range(TT)] for n in "ABC"}
        side = [ctx.enter_context(nc.psum_tensor(f"side{b}", [P, COL], F32)) for b in range(2)]

        w_landed = [sem(f"w_landed{s}") for s in range(RAW)]
        w_first = sem("w_first")
        gain_landed = sem("gain_landed")
        x_landed = [sem(f"x_landed{c}") for c in range(NC)]
        p_landed = sem("p_landed")
        rope_landed = sem("rope_landed")
        dec_landed = sem("dec_landed")
        idn_landed = sem("idn_landed")
        pscale_landed = sem("pscale_landed")
        band_landed = sem("band_landed")
        inv_landed = sem("inv_landed")
        fgain_landed = sem("fgain_landed")
        stored = sem("stored")
        hi_ready = sem("hi_ready")
        lo_ready = sem("lo_ready")
        unit_used = sem("unit_used")
        p_hi = sem("p_hi")
        p_split = sem("p_split")
        hT_done = sem("hT_done")
        hT_hi = sem("hT_hi")
        xT_ready = sem("xT_ready")
        ssq_ready = sem("ssq_ready")
        rs_ready = sem("rs_ready")
        qk_read = sem("qk_read")
        qk_ready = sem("qk_ready")
        qkT_done = sem("qkT_done")
        qkT_hi_ready = sem("qkT_hi_ready")
        qkT_ready = sem("qkT_ready")
        st_done = sem("st_done")
        pr_whole = sem("pr_whole")
        pr_hi_ready = sem("pr_hi_ready")
        pr_ready = sem("pr_ready")
        v_hi_ready = sem("v_hi_ready")
        v_ready = sem("v_ready")
        y_done = sem("y_done")
        sig_ready = sem("sig_ready")
        g_read = sem("g_read")
        y_gated = sem("y_gated")
        yT_done = sem("yT_done")
        yT_hi = sem("yT_hi")
        yT_ready = sem("yT_ready")
        o_read = sem("o_read")
        e_read = sem("e_read")
        z_read = sem("z_read")
        h_ready = sem("h_ready")
        band_ready = sem("band_ready")
        u_hi_ready = sem("u_hi_ready")
        u_ready = sem("u_ready")
        band_done = sem("band_done")
        d_scaled = sem("d_scaled")
        d_hi_ready = sem("d_hi_ready")
        d_ready = sem("d_ready")
        psig_ready = sem("psig_ready")
        pg_ready = sem("pg_ready")
        m_ready = sem("m_ready")
        mT_done = sem("mT_done")
        mT_hi = sem("mT_hi")
        mT_ready = sem("mT_ready")
        fin_ready = sem("fin_ready")
        out_v = sem("out_v")
        out_a = sem("out_a")
        tile_done = sem("tile_done")
        z_tile = sem("z_tile")
        ssq_tile = sem("ssq_tile")
        rs_tile = sem("rs_tile")
        fin_tile = sem("fin_tile")
        h_tile = sem("h_tile")
        dve_step = sem("dve_step")

        block = ctx.enter_context(nc.Block())

        @block.sync
        def _(sp):
            def x_chunk(c):
                sp.dma_start(h[:, :, c * COL:(c + 1) * COL],
                             x[:, c * COL:(c + 1) * COL].rearrange("(t p) d -> p t d", p=P)).then_inc(x_landed[c], 16)

            def piece(s):
                sp.dma_start(w_raw[:, s, :], stream[s, :, :]).then_inc(w_landed[s], 16)

            x_chunk(0)
            sp.dma_start(gain[:], gains).then_inc(gain_landed, 16)
            sp.dma_start(w_raw[:, 0, 0:UNIT * COL], stream[0, :, 0:UNIT * COL]).then_inc(w_first, 16)
            sp.dma_start(w_raw[:, 0, UNIT * COL:], stream[0, :, UNIT * COL:]).then_inc(w_landed[0], 16)
            for c in range(1, NC):
                x_chunk(c)
                piece(c)
            rounds = stream.rearrange("(i s) p n -> i s p n", s=RAW)
            with sp.Fori(1, PIECES // RAW) as i:
                for s in range(RAW):
                    sp.wait_ge(lo_ready, i * (2 * RAW) + (2 * s + 2 - 2 * RAW))
                    sp.dma_start(w_raw[:, s, :], rounds[i, s, :, :]).then_inc(w_landed[s], 16)
            for t in range(TT):
                sp.wait_ge(out_v, (t + 1) * (NC - ACT_OUT))
                sp.dma_start(out[t * P:(t + 1) * P, 0:D - ACT_OUT * COL], emb[:, t, 0:D - ACT_OUT * COL]
                             ).then_inc(stored, 16)
            sp.wait_ge(stored, 2 * TT * 16)

        @block.gpsimd
        def _(pool):
            pool.dma_start(idn[:], ident).then_inc(idn_landed, 16)
            pool.dma_start(pscale[:], pool_scale).then_inc(pscale_landed, 16)
            pool.wait_ge(x_landed[NC - 1], 16)
            pool.dma_start(ropec[:], rope[0]).then_inc(rope_landed, 16)
            pool.dma_start(ropes[:], rope[1]).then_inc(rope_landed, 16)
            pool.dma_start(dec[:], decay).then_inc(dec_landed, 16)
            pool.dma_start(p_raw, pT).then_inc(p_landed, 16)
            pool.wait_ge(yT_done, HEADS)
            pool.dma_start(bnd_raw[:], band).then_inc(band_landed, 16)
            pool.dma_start(inv[:], counts).then_inc(inv_landed, 16)
            pool.wait_ge(d_ready, 2 * GROUPS)
            pool.dma_start(fgain[:], final_gain).then_inc(fgain_landed, 16)

        @block.tensor
        def _(pe):
            def products(t, s, pair, hi, lo, k0, first, last):
                for b in range(UNIT):
                    xh = hi[:, k0 + b, t * P:(t + 1) * P]
                    xl = lo[:, k0 + b, t * P:(t + 1) * P]
                    wh = w_hi[:, s, b * COL:(b + 1) * COL]
                    wl = w_lo[:, s, b * COL:(b + 1) * COL]
                    pe.matmul(acc[pair][t][:], xh, wh, start=first and b == 0, stop=False)
                    pe.matmul(acc[pair][t][:], xh, wl, start=False, stop=False)
                    mm = pe.matmul(acc[pair][t][:], xl, wh, start=False, stop=last and b == UNIT - 1)
                return mm

            def unit(u, base, pair, hi, lo, k0, first, last, seg=0):
                pe.wait_ge(lo_ready, base + (u + 1))
                for t in range(TT):
                    mm = products(t, (seg + u) % RING, pair, hi, lo, k0, first, last)
                mm.then_inc(unit_used, 1)

            def wide(u, base, k, pair, hi, lo, stage=None):
                if stage is not None and k % 2 == 0:
                    pe.wait_ge(xT_ready, NC * stage + k // 2 + 1)
                unit(u, base, pair, hi, lo, k * UNIT, k == 0, k == KD_U - 1)

            def transpose4(src, tiles):
                for j in range(4):
                    for t in range(TT):
                        mm = pe.transpose(side[j // 2][:, (j % 2) * SEQ + t * P:(j % 2) * SEQ + (t + 1) * P],
                                          src(t)[:, tiles + j * P:tiles + (j + 1) * P], idn[:])
                return mm

            def h_transposes(stage, c):
                if stage == 0:
                    pe.wait_ge(x_landed[c], 16)
                else:
                    pe.wait_ge(h_ready, NC * (stage - 1) + c + 1)
                if stage + c > 0:
                    pe.wait_ge(xT_ready, NC * stage + c)
                transpose4(lambda t: h[:, t, :], c * COL).then_inc(hT_done, 1)

            def y_transposes(hd):
                pe.wait_ge(y_gated, hd + 1)
                transpose4(lambda t: yn[:, t, :], 0).then_inc(yT_done, 1)

            def qk_transposes(hd):
                pe.wait_ge(qk_ready, hd + 1)
                transpose4(lambda t: qk[:, t, :], 0).then_inc(qkT_done, 1)

            def scores(hd):
                pe.wait_ge(qkT_ready, hd + 1)
                for keys, queries, o in ((slice(0, P), slice(0, SEQ), 0), (slice(P, SEQ), slice(P, SEQ), SEQ)):
                    for j in range(2):
                        st = side[0][:, o:o + queries.stop - queries.start]
                        kh, kl = qkT_hi[:, 2 + j, keys], qkT_lo[:, 2 + j, keys]
                        qh, ql = qkT_hi[:, j, queries], qkT_lo[:, j, queries]
                        pe.matmul(st, kh, qh, start=j == 0, stop=False)
                        pe.matmul(st, kh, ql, start=False, stop=False)
                        mm = pe.matmul(st, kl, qh, start=False, stop=j == 1)
                mm.then_inc(st_done, 1)

            def values(hd):
                pe.wait_ge(pr_ready, hd + 1)
                pe.wait_ge(v_ready, hd + 1)
                for b, cols, t, a, e in ((0, slice(0, P), 0, True, True), (1, slice(P, SEQ), 0, True, False),
                                         (1, slice(SEQ, SEQ + P), 1, False, True)):
                    pe.matmul(side[b][:], pr_hi[:, cols], v_hi[:, t, :], start=a, stop=False)
                    pe.matmul(side[b][:], pr_hi[:, cols], v_lo[:, t, :], start=False, stop=False)
                    mm = pe.matmul(side[b][:], pr_lo[:, cols], v_hi[:, t, :], start=False, stop=e)
                mm.then_inc(y_done, 1)

            def head(hd, base, first):
                o = 0 if first else NC * RO_U
                if not first:
                    pe.wait_ge(qk_read, hd)
                for u in range(KD_U):
                    wide(u, base, u, "A", xa_hi, xa_lo, 0 if first else None)
                    if first and u + 2 < NC:
                        h_transposes(0, u + 2)
                    if u == 3 and not first:
                        y_transposes(hd - 1)
                if not first:
                    pe.wait_ge(yT_ready, hd)
                    for c in range(NC):
                        if c == 0:
                            pe.wait_ge(g_read, hd)
                        if c == 1:
                            pe.wait_ge(v_ready, hd)
                        if c == 2:
                            pe.wait_ge(qk_read, hd + 1)
                        if c == 3:
                            pe.wait_ge(o_read, hd * NC - (NC - 1))
                        for k in range(RO_U):
                            unit(KD_U + c * RO_U + k, base, "BCAB"[c], oT_hi, oT_lo, k * UNIT, k == 0, k == RO_U - 1)
                    pe.wait_ge(o_read, hd * NC - 2)
                for u in range(KD_U):
                    wide(KD_U + o + u, base, u, "C", xa_hi, xa_lo)
                    if u == 1:
                        qk_transposes(hd)
                    if u == 5:
                        scores(hd)
                if not first:
                    pe.wait_ge(o_read, hd * NC)
                for u in range(KD_U):
                    wide(2 * KD_U + o + u, base, u, "B", xa_hi, xa_lo)
                    if u == 4:
                        values(hd)

            def window_sums(g, n, c):
                pe.wait_ge(u_ready, n + 1)
                for j in range(4):
                    ch = slice(j * P, (j + 1) * P)
                    o = (j % 2) * SEQ
                    pe.matmul(side[j // 2][:, o:o + SEQ], u_hi[:, 0, ch], bnd[:, g, 0:SEQ], start=True, stop=False)
                    pe.matmul(side[j // 2][:, o:o + SEQ], u_lo[:, 0, ch], bnd[:, g, 0:SEQ], start=False, stop=False)
                    pe.matmul(side[j // 2][:, o + P:o + SEQ], u_hi[:, 1, ch], bnd[:, g, SEQ:SEQ + P],
                              start=False, stop=False)
                    mm = pe.matmul(side[j // 2][:, o + P:o + SEQ], u_lo[:, 1, ch], bnd[:, g, SEQ:SEQ + P],
                                   start=False, stop=True)
                mm.then_inc(band_done, 1)

            def m_transposes(n, c):
                pe.wait_ge(m_ready, n + 1)
                transpose4(lambda t: gm[:, c, t, :], 0).then_inc(mT_done, 1)

            def group(g, base, first, seg):
                o = 0 if first else NC * PO_U
                n2 = g * 2
                if not first:
                    pe.wait_ge(pg_ready, n2 - 1)
                for k in range(KD_U):
                    if first and k % 2 == 0:
                        pe.wait_ge(xT_ready, NC * 2 + k // 2 + 1)
                    unit(k, base, "A", xa_hi, xa_lo, k * UNIT, k == 0, k == KD_U - 1, seg)
                    if first and k == 1:
                        h_transposes(2, NC - 1)
                    if not first and k == 3:
                        pe.wait_ge(mT_ready, n2 - 1)
                        m_transposes(n2 - 1, 1)
                if not first:
                    pe.wait_ge(mT_ready, n2)
                    pe.wait_ge(m_ready, n2)
                    for c in range(NC):
                        if c == 2:
                            pe.wait_ge(u_ready, n2 + 1)
                        if c == 3:
                            pe.wait_ge(o_read, g * NC + (O_RET + 1))
                        for k in range(PO_U):
                            unit(KD_U + c * PO_U + k, base, "BCAB"[c], oT_hi, oT_lo, k * UNIT, k == 0,
                                 k == PO_U - 1, seg)
                            if c == 1 and k == 1:
                                window_sums(g, n2, 0)
                    pe.wait_ge(o_read, g * NC + (O_RET + 2))
                else:
                    pe.wait_ge(z_read, NC)
                for k in range(KD_U):
                    unit(KD_U + o + k, base, "C", xa_hi, xa_lo, k * UNIT, k == 0, k == KD_U - 1, seg)
                    if first and k == 5:
                        pe.wait_ge(band_ready, 1)
                        window_sums(g, n2, 0)
                if first:
                    pe.wait_ge(u_ready, n2 + 1)
                else:
                    pe.wait_ge(o_read, g * NC + (O_RET + 3))
                for k in range(KD_U):
                    unit(2 * KD_U + o + k, base, "A", xa_hi, xa_lo, k * UNIT, k == 0, k == KD_U - 1, seg)
                    if k == 5:
                        pe.wait_ge(d_scaled, n2 * 2 + 2)
                        window_sums(g, n2 + 1, 1)
                if not first:
                    pe.wait_ge(o_read, g * NC + (O_RET + NC))
                for k in range(KD_U):
                    unit(3 * KD_U + o + k, base, "B", xa_hi, xa_lo, k * UNIT, k == 0, k == KD_U - 1, seg)
                pe.wait_ge(d_ready, n2 + 2)
                pe.wait_ge(u_ready, n2 + 2)
                for k in range(PO_U):
                    unit(4 * KD_U + o + k, base, "C", dT_hi, dT_lo, k * UNIT, k == 0, k == PO_U - 1, seg)
                pe.wait_ge(pg_ready, n2 + 2)
                for k in range(PO_U):
                    unit(4 * KD_U + PO_U + o + k, base, "B", dT_hi, dT_lo, k * UNIT, k == 0, k == PO_U - 1, seg)
                    if k == 1:
                        m_transposes(n2, 0)

            def close(layer, base, seg, ou):
                for c in range(EMB_U):
                    if c >= 2:
                        pe.wait_ge(e_read, layer * NC + c - 1)
                    if c == 1 and layer == 0:
                        pe.wait_ge(v_ready, HEADS)
                    if c == 0 and layer == 0:
                        pe.wait_ge(p_split, 1)
                    unit(c, base, "AC"[c % 2], pT_hi[:, layer], pT_lo[:, layer], 0, True, True, seg)
                    if c == 2 and layer == 0:
                        y_transposes(HEADS - 1)
                    if c == 2 and layer == 1:
                        pe.wait_ge(mT_ready, 2 * GROUPS - 1)
                        m_transposes(2 * GROUPS - 1, 1)
                if layer == 0:
                    pe.wait_ge(g_read, HEADS)
                    pe.wait_ge(yT_ready, HEADS)
                else:
                    pe.wait_ge(m_ready, 2 * GROUPS)
                    pe.wait_ge(mT_ready, 2 * GROUPS)
                h0 = 2 * layer * NC
                z0 = layer * NC
                last = EMB_U + NC * ou + GATE_U
                if layer == 1:
                    last -= RING
                for u in range(EMB_U, last):
                    c, k = divmod(u - EMB_U, ou)
                    z, kz = divmod(u - EMB_U - NC * ou, KD_U)
                    if c < NC:
                        if k == 0 and c in (1, 2):
                            pe.wait_ge(e_read, z0 + c + 2)
                        if k == 0 and c == 3:
                            pe.wait_ge(h_ready, h0 + 1)
                        unit(u, base, "BACB"[c], oT_hi, oT_lo, k * UNIT, k == 0, k == ou - 1, seg)
                    else:
                        if kz == 0 and z < 3:
                            pe.wait_ge(h_ready, h0 + z + 2)
                        if kz == 0 and z == 3:
                            pe.wait_ge(z_read, z0 + 2)
                        if z == 0 and kz % 2 == 0:
                            pe.wait_ge(xT_ready, NC * (2 * layer + 1) + kz // 2 + 1)
                        unit(u, base, "ACBC"[z], xb_hi, xb_lo, kz * UNIT, kz == 0, kz == KD_U - 1, seg)
                    for cc in range(NC):
                        if u == EMB_U + ou * (cc + 1):
                            h_transposes(2 * layer + 1, cc)
                        if cc < NC - 1 and layer == 0 and u == EMB_U + NC * ou + KD_U * (cc + 1) + 1:
                            h_transposes(2, cc)

            pe.wait_ge(idn_landed, 16)
            h_transposes(0, 0)
            h_transposes(0, 1)
            head(0, RET0, True)
            with pe.Fori(1, HEADS) as hd:
                head(hd, hd * HEAD_U + (RET1 - HEAD_U), False)
            close(0, CLOSE_A, CLOSE_A % RING, RO_U)
            group(0, POOL0, True, POOL0 % RING)
            with pe.Fori(1, GROUPS) as g:
                group(g, g * GROUP_U + (POOL1 - GROUP_U), False, POOL1 % RING)
            close(1, CLOSE_B, CLOSE_B % RING, PO_U)
            for t in range(TT):
                for k in range(KD_U - RING, KD_U):
                    if t == 0:
                        pe.wait_ge(lo_ready, UNITS - KD_U + k + 1)
                    mm = products(t, (UNITS - KD_U + k) % RING, "C", xb_hi, xb_lo, k * UNIT, False, k == KD_U - 1)
                mm.then_inc(tile_done, 1)

        @block.scalar
        def _(act):
            def split_hi(u, base, seg, landings):
                r = (seg + u) % (2 * RAW)
                if isinstance(base, int) and base + u == 0:
                    act.wait_ge(w_first, 16)
                elif u % 2 == 0 or (isinstance(base, int) and base + u == 1):
                    act.wait_ge(w_landed[r // 2], landings(u))
                if not (isinstance(base, int) and base + u < RING):
                    act.wait_ge(unit_used, base + (u + 1 - RING))
                act.copy(w_hi[:, r % RING, :], w_raw[:, r // 2, (r % 2) * 1024:(r % 2 + 1) * 1024]).then_inc(hi_ready, 1)

            def landed(base):
                return lambda u: ((base + u) // (2 * RAW) + 1) * 16

            def squares(stage, c):
                if stage * NC + c:
                    act.wait_ge(ssq_ready, stage * NC + c)
                for t in range(TT):
                    sq = act.activation(junk[:, t, :], h[:, t, c * COL:(c + 1) * COL],
                                        ACT.Square, accum_out=ssq[:, stage, t, c:c + 1])
                sq.then_inc(ssq_ready, 1)

            def stream_hi(stage, c):
                hi = xb_hi if stage % 2 else xa_hi
                act.wait_ge(hT_done, NC * stage + c + 1)
                for j in range(4):
                    k = 4 * c + j
                    cp = act.activation(hi[:, k, :], side[j // 2][:, (j % 2) * SEQ:(j % 2 + 1) * SEQ], ACT.Copy,
                                        scale=gain[:, stage, k:k + 1])
                    if j % 2:
                        cp.then_inc(hT_hi, 1)

            def v_hi_part(hd, done):
                act.wait_ge(unit_used, done)
                for t in range(TT):
                    act.activation(v_hi[:, t, :], acc["C"][t][:], ACT.Copy, scale=rs[:, 0, t:t + 1]).then_inc(v_hi_ready, 1)

            def pr_hi_part(hd):
                act.wait_ge(pr_whole, hd + 1)
                act.copy(pr_hi[:], pr[:]).then_inc(pr_hi_ready, 1)

            def qkT_hi_part(hd):
                act.wait_ge(qkT_done, hd + 1)
                for b in range(2):
                    act.copy(qkT_hi[:, 2 * b:2 * b + 2, :], side[b][:].rearrange("p (k n) -> p k n", n=SEQ)
                             ).then_inc(qkT_hi_ready, 1)

            def g_sigmoid(hd, done):
                act.wait_ge(unit_used, done)
                for t in range(TT):
                    act.activation(sig[:, t, :], acc["B"][t][:], ACT.Sigmoid, scale=rs[:, 0, t:t + 1]).then_inc(sig_ready, 1)

            def y_hi_part(hd):
                act.wait_ge(yT_done, hd + 1)
                for b in range(2):
                    act.copy(oT_hi[:, 2 * b:2 * b + 2, :], side[b][:].rearrange("p (k n) -> p k n", n=SEQ)
                             ).then_inc(yT_hi, 1)

            def emb_out(layer, c, base):
                act.wait_ge(unit_used, base + c + 1)
                for t in range(TT):
                    cp = act.copy(emb[:, t, c * COL:(c + 1) * COL], acc["AC"[c % 2]][t][:])
                cp.then_inc(e_read, 1)

            def z_sigmoid(layer, c, done):
                act.wait_ge(unit_used, done)
                for t in range(TT):
                    sg = act.activation(sig[:, t, :], acc["ACBC"[c]][t][:], ACT.Sigmoid,
                                        scale=rs[:, 2 * layer + 1, t:t + 1])
                sg.then_inc(z_read, 1)

            def finished(n, stage):
                act.wait_ge(h_ready, n + 1)
                squares(stage, n % NC)

            def u_hi_part(n, pair, done):
                act.wait_ge(unit_used, done)
                for t in range(TT):
                    act.activation(u_hi[:, t, :], acc[pair][t][:], ACT.Copy, scale=rs[:, 2, t:t + 1]).then_inc(u_hi_ready, 1)

            def d_hi_part(n, c):
                for b in range(2):
                    act.wait_ge(d_scaled, n * 2 + (b + 1))
                    act.copy(dT_hi[:, 4 * c + 2 * b:4 * c + 2 * b + 2, :], d_tmp[:, 2 * b:2 * b + 2, :]).then_inc(d_hi_ready, 1)

            def pg_sigmoid(n, pair, done, first):
                act.wait_ge(unit_used, done)
                if not first:
                    act.wait_ge(pg_ready, n)
                for t in range(TT):
                    act.activation(sig[:, t, :], acc[pair][t][:], ACT.Sigmoid, scale=rs[:, 2, t:t + 1]).then_inc(psig_ready, 1)

            def m_hi_part(n, k0, c):
                act.wait_ge(mT_done, n + 1)
                for j in range(4):
                    cp = act.activation(oT_hi[:, 4 * c + j, :], side[j // 2][:, (j % 2) * SEQ:(j % 2 + 1) * SEQ], ACT.Copy,
                                        scale=pscale[:, bass.ds(k0 + j, 1)])
                    if j % 2:
                        cp.then_inc(mT_hi, 1)

            def head(hd, base, first, landings):
                o = 0 if first else NC * RO_U
                for u in range(3 * KD_U + o):
                    split_hi(u, base, RET1 % (2 * RAW) if not first else 0, landings)
                    if first and u + 1 < NC:
                        stream_hi(0, u + 1)
                    if first and 6 <= u < 6 + NC:
                        squares(0, u - 6)
                    if first and u == 14:
                        act.wait_ge(p_landed, 16)
                        act.copy(pT_hi[:], p_raw).then_inc(p_hi, 1)
                    if not first and u == 2:
                        g_sigmoid(hd - 1, base)
                    if not first and u == 6:
                        y_hi_part(hd - 1)
                    if u == KD_U + o + 4:
                        qkT_hi_part(hd)
                    if u == 2 * KD_U + o:
                        pr_hi_part(hd)
                    if u == 2 * KD_U + o + 2:
                        if first:
                            act.wait_ge(rs_ready, 1)
                        v_hi_part(hd, base + (2 * KD_U + o))

            def group(g, base, first, seg, landings):
                o = 0 if first else NC * PO_U
                n2 = g * 2
                for u in range(4 * KD_U + 2 * PO_U + o):
                    split_hi(u, base, seg, landings)
                    if first and u == 2:
                        z_sigmoid(0, NC - 1, base)
                        finished(2 * NC - 1, 2)
                    if first and u == 4:
                        stream_hi(2, NC - 1)
                    if not first and u == 0:
                        m_hi_part(n2 - 2, g * KG - KG, 0)
                    if not first and u == 6:
                        m_hi_part(n2 - 1, g * KG - KG // 2, 1)
                    if u == KD_U + 2:
                        if first:
                            act.wait_ge(rs_ready, 3)
                        u_hi_part(n2, "A", base + KD_U)
                    if u == (KD_U + 8 if first else KD_U + PO_U + 4):
                        d_hi_part(n2, 0)
                    if u == 2 * KD_U + o + 2:
                        u_hi_part(n2 + 1, "C", base + (2 * KD_U + o))
                    if u == 2 * KD_U + o + 8:
                        d_hi_part(n2 + 1, 1)
                    if u == 3 * KD_U + o + 2:
                        pg_sigmoid(n2, "A", base + (3 * KD_U + o), first)
                    if u == 4 * KD_U + o + 2:
                        pg_sigmoid(n2 + 1, "B", base + (4 * KD_U + o), False)

            def close(layer, base, ou):
                seg = base % (2 * RAW)
                for u in range(EMB_U + NC * ou + GATE_U):
                    split_hi(u, base, seg, landed(base))
                    if u == 0 and layer == 1:
                        m_hi_part(2 * GROUPS - 2, (GROUPS - 1) * KG, 0)
                    if u == 2 and layer == 0:
                        g_sigmoid(HEADS - 1, base)
                    if u == 5:
                        if layer == 0:
                            y_hi_part(HEADS - 1)
                        else:
                            m_hi_part(2 * GROUPS - 1, (GROUPS - 1) * KG + KG // 2, 1)
                    for c in range(NC):
                        if u == c + 3:
                            emb_out(layer, c, base)
                        if u == EMB_U + NC * ou + 4 + c:
                            finished(2 * layer * NC + c, 2 * layer + 1)
                        if u == EMB_U + ou * (c + 1) + 3:
                            stream_hi(2 * layer + 1, c)
                        z = EMB_U + NC * ou + KD_U * (c + 1)
                        if u == z + 2:
                            if c == 0:
                                act.wait_ge(rs_ready, 2 * layer + 2)
                            z_sigmoid(layer, c, base + z)
                            finished((2 * layer + 1) * NC + c, 2 * layer + 2)
                        if u == z + 4 and layer == 0:
                            stream_hi(2, c)
                    if u == EMB_U + NC * ou + 14 and layer == 0:
                        act.wait_ge(band_landed, 16)
                        act.copy(bnd[:], bnd_raw[:]).then_inc(band_ready, 1)

            act.wait_ge(idn_landed, 16)
            act.activation(warm[:], idn[:, 0:1], ACT.Sigmoid)
            act.wait_ge(gain_landed, 16)
            stream_hi(0, 0)
            head(0, RET0, True, landed(0))
            with act.Fori(1, HEADS) as hd:
                head(hd, hd * HEAD_U + (RET1 - HEAD_U), False,
                     lambda u: hd * (HEAD_U // 8 * 16) + ((RET1 - HEAD_U + u) // 8 + 1) * 16)
            close(0, CLOSE_A, RO_U)
            act.wait_ge(pscale_landed, 16)
            group(0, POOL0, True, POOL0 % 8, landed(POOL0))
            with act.Fori(1, GROUPS) as g:
                group(g, g * GROUP_U + (POOL1 - GROUP_U), False, POOL1 % 8,
                      lambda u: g * (GROUP_U // 8 * 16) + ((POOL1 - GROUP_U + u) // 8 + 1) * 16)
            close(1, CLOSE_B, PO_U)
            def last_sigmoid(t):
                act.wait_ge(tile_done, t + 1)
                act.activation(sig[:, t, :], acc["C"][t][:], ACT.Sigmoid, scale=rs[:, 3, t:t + 1]).then_inc(z_tile, 1)

            def last_squares(t):
                act.wait_ge(h_tile, t + 1)
                act.activation(junk[:, t, :], h[:, t, D - COL:D], ACT.Square, accum_out=ssq[:, 4, t, NC - 1:NC]
                               ).then_inc(ssq_tile, 1)

            def last_out(t):
                act.wait_ge(rs_tile, t + 1)
                act.wait_ge(fin_tile, t + 1)
                for c in range(NC - ACT_OUT, NC):
                    act.activation(emb[:, t, c * COL:(c + 1) * COL], emb[:, t, c * COL:(c + 1) * COL], ACT.Copy,
                                   scale=rs[:, 4, t:t + 1]).then_inc(out_a, 1)
                act.wait_ge(out_a, (t + 1) * ACT_OUT)
                act.dma_start(out[t * P:(t + 1) * P, D - ACT_OUT * COL:D], emb[:, t, D - ACT_OUT * COL:D]
                              ).then_inc(stored, 16)

            last_sigmoid(0)
            act.wait_ge(ssq_ready, STAGES * NC - 1)
            last_squares(0)
            last_sigmoid(1)
            last_out(0)
            last_squares(1)
            last_out(1)

        @block.vector
        def _(dve):
            own = Steps(dve, dve_step)

            def split_lo(u, base, seg):
                r = (seg + u) % (2 * RAW)
                dve.wait_ge(hi_ready, base + (u + 1))
                dve.tensor_tensor(w_lo[:, r % RING, :], w_raw[:, r // 2, (r % 2) * 1024:(r % 2 + 1) * 1024],
                                  w_hi[:, r % RING, :].bitcast(F32), ALU.subtract).then_inc(lo_ready, 1)

            def rsqrt(dst, src, scale, eps):
                w = dst.shape[-1]
                nx, nt, ni = (a[:, 0:w] for a in (nx2, nt2, ni2))
                own.mark(dve.tensor_scalar(nx, src, scale, eps, ALU.mult, ALU.add))
                own.wait()
                own.mark(dve.tensor_scalar(ni, nx.bitcast(I32), 1, None, ALU.logical_shift_right))
                own.wait()
                own.mark(dve.tensor_scalar(dst.bitcast(I32), ni, -1, MAGIC, ALU.mult, ALU.add))
                own.wait()
                for i in range(NEWTON):
                    own.mark(dve.scalar_tensor_tensor(out=nt, in0=dst, scalar=-0.5, in1=nx, op0=ALU.mult, op1=ALU.mult))
                    own.wait()
                    own.mark(dve.tensor_tensor(nt, nt, dst, ALU.mult))
                    own.wait()
                    ins = dve.scalar_tensor_tensor(out=dst, in0=nt, scalar=1.5, in1=dst, op0=ALU.add, op1=ALU.mult)
                    if i < NEWTON - 1:
                        own.mark(ins)
                        own.wait()
                return ins

            def row_scale(stage):
                dve.wait_ge(ssq_ready, NC * (stage + 1))
                own.mark(dve.tensor_reduce(rstd[:], ssq[:, stage, :, :], AX.X, ALU.add))
                own.wait()
                rsqrt(rs[:, stage, :], rstd[:], 1.0 / D, NORM_EPS).then_inc(rs_ready, 1)
                dve.wait_ge(rs_ready, stage + 1)

            def stream_lo(stage, c):
                hi, lo = (xb_hi, xb_lo) if stage % 2 else (xa_hi, xa_lo)
                for j in range(4):
                    k = 4 * c + j
                    if j % 2 == 0:
                        dve.wait_ge(hT_hi, 2 * (NC * stage + c) + j // 2 + 1)
                    ins = dve.scalar_tensor_tensor(
                        out=lo[:, k, :], in0=side[j // 2][:, (j % 2) * SEQ:(j % 2 + 1) * SEQ],
                        scalar=gain[:, stage, k:k + 1], in1=hi[:, k, :].bitcast(F32), op0=ALU.mult, op1=ALU.subtract)
                ins.then_inc(xT_ready, 1)

            def rotate(hd, done):
                dve.wait_ge(unit_used, done)
                for t in range(TT):
                    dve.scalar_tensor_tensor(out=qk[:, t, :], in0=acc["A"][t][:], scalar=rs[:, 0, t:t + 1],
                                             in1=ropec[:, t, :], op0=ALU.mult, op1=ALU.mult)
                    swapped = acc["A"][t][:].rearrange("p (i two) -> p i two", two=2)[:, :, ::-1]
                    ins = dve.scalar_tensor_tensor(
                        out=qk2[:, t, :].rearrange("p (i two) -> p i two", two=2), in0=swapped,
                        scalar=rs[:, 0, t:t + 1], in1=ropes[:, t, :].rearrange("p (i two) -> p i two", two=2),
                        op0=ALU.mult, op1=ALU.mult)
                ins.then_inc(qk_read, 1)
                dve.wait_ge(qk_read, hd + 1)
                dve.tensor_tensor(qk[:], qk[:], qk2[:], ALU.add).then_inc(qk_ready, 1)

            def decay_scores(hd):
                dve.wait_ge(st_done, hd + 1)
                dve.tensor_tensor(pr[:, 0:SEQ], side[0][:, 0:SEQ], dec[:, hd, :], ALU.mult)
                dve.tensor_tensor(pr[:, SEQ:SEQ + P], side[0][:, SEQ:SEQ + P], dec[:, hd, 0:P], ALU.mult).then_inc(pr_whole, 1)

            def pr_lo_part(hd):
                dve.wait_ge(pr_hi_ready, hd + 1)
                dve.tensor_tensor(pr_lo[:], pr[:], pr_hi[:].bitcast(F32), ALU.subtract).then_inc(pr_ready, 1)

            def qkT_lo_part(hd):
                for b in range(2):
                    dve.wait_ge(qkT_hi_ready, hd * 2 + (b + 1))
                    ins = dve.tensor_tensor(qkT_lo[:, 2 * b:2 * b + 2, :], side[b][:].rearrange("p (k n) -> p k n", n=SEQ),
                                            qkT_hi[:, 2 * b:2 * b + 2, :].bitcast(F32), ALU.subtract)
                ins.then_inc(qkT_ready, 1)

            def v_lo_part(hd):
                for t in range(TT):
                    dve.wait_ge(v_hi_ready, hd * 2 + (t + 1))
                    ins = dve.scalar_tensor_tensor(out=v_lo[:, t, :], in0=acc["C"][t][:], scalar=rs[:, 0, t:t + 1],
                                                   in1=v_hi[:, t, :].bitcast(F32), op0=ALU.mult, op1=ALU.subtract)
                ins.then_inc(v_ready, 1)

            def normalise(hd):
                dve.wait_ge(y_done, hd + 1)
                for t in range(TT):
                    ins = dve.bn_stats(stats[:, t, :], side[t][:])
                own.mark(ins)
                own.wait()
                dve.memset(nt2[:], 0.0)
                for t in range(TT):
                    ins = dve.bn_aggr(mv[:, t, :], stats[:, t, :])
                own.mark(ins)
                own.wait()
                own.mark(rsqrt(rstd[:], mv[:, :, 1], 1.0, GN_EPS))
                own.wait()
                for t in range(TT):
                    ins = dve.tensor_scalar(yn[:, t, :], side[t][:], mv[:, t, 0:1], rstd[:, t:t + 1], ALU.subtract, ALU.mult)
                own.mark(ins)

            def gate_y(hd):
                for t in range(TT):
                    dve.wait_ge(sig_ready, hd * 2 + (t + 1))
                    ins = dve.scalar_tensor_tensor(out=sig[:, t, :], in0=acc["B"][t][:], scalar=rs[:, 0, t:t + 1],
                                                   in1=sig[:, t, :], op0=ALU.mult, op1=ALU.mult)
                ins.then_inc(g_read, 1)
                dve.wait_ge(g_read, hd + 1)
                own.wait()
                dve.tensor_tensor(yn[:], yn[:], sig[:], ALU.mult).then_inc(y_gated, 1)

            def y_lo_part(hd):
                for b in range(2):
                    dve.wait_ge(yT_hi, hd * 2 + (b + 1))
                    ins = dve.tensor_tensor(oT_lo[:, 2 * b:2 * b + 2, :], side[b][:].rearrange("p (k n) -> p k n", n=SEQ),
                                            oT_hi[:, 2 * b:2 * b + 2, :].bitcast(F32), ALU.subtract)
                ins.then_inc(yT_ready, 1)

            def add_gated(n):
                layer, c = n // NC, n % NC
                dve.wait_ge(z_read, n + 1)
                own.mark(dve.tensor_tensor(sig[:], sig[:], emb[:, :, c * COL:(c + 1) * COL], ALU.mult))
                own.wait()
                dve.tensor_tensor(h[:, :, c * COL:(c + 1) * COL], h[:, :, c * COL:(c + 1) * COL], sig[:], ALU.add
                                  ).then_inc(h_ready, 1)

            def u_lo_part(n, pair):
                for t in range(TT):
                    dve.wait_ge(u_hi_ready, n * 2 + (t + 1))
                    ins = dve.scalar_tensor_tensor(out=u_lo[:, t, :], in0=acc[pair][t][:], scalar=rs[:, 2, t:t + 1],
                                                   in1=u_hi[:, t, :].bitcast(F32), op0=ALU.mult, op1=ALU.subtract)
                ins.then_inc(u_ready, 1)

            def d_scale(g, n):
                dve.wait_ge(band_done, n + 1)
                for b in range(2):
                    dve.tensor_tensor(d_tmp[:, 2 * b:2 * b + 2, :], side[b][:].rearrange("p (k n) -> p k n", n=SEQ),
                                      inv[:, bass.ds(g, 1), :].to_broadcast([P, 2, SEQ]), ALU.mult).then_inc(d_scaled, 1)

            def d_lo_part(n, c):
                for b in range(2):
                    dve.wait_ge(d_hi_ready, n * 2 + (b + 1))
                    ks = slice(4 * c + 2 * b, 4 * c + 2 * b + 2)
                    ins = dve.tensor_tensor(dT_lo[:, ks, :], d_tmp[:, 2 * b:2 * b + 2, :], dT_hi[:, ks, :].bitcast(F32),
                                            ALU.subtract)
                ins.then_inc(d_ready, 1)

            def gate_p(n, c, pair):
                for t in range(TT):
                    dve.wait_ge(psig_ready, n * 2 + (t + 1))
                    ins = dve.scalar_tensor_tensor(out=gm[:, c, t, :], in0=acc[pair][t][:], scalar=rs[:, 2, t:t + 1],
                                                   in1=sig[:, t, :], op0=ALU.mult, op1=ALU.mult)
                ins.then_inc(pg_ready, 1)

            def mix(n, c, pair, done):
                dve.wait_ge(unit_used, done)
                for t in range(TT):
                    ins = dve.tensor_tensor(gm[:, c, t, :], acc[pair][t][:], gm[:, c, t, :], ALU.mult)
                ins.then_inc(m_ready, 1)

            def m_lo_part(n, k0, c):
                for j in range(4):
                    if j % 2 == 0:
                        dve.wait_ge(mT_hi, n * 2 + (j // 2 + 1))
                    ins = dve.scalar_tensor_tensor(
                        out=oT_lo[:, 4 * c + j, :], in0=side[j // 2][:, (j % 2) * SEQ:(j % 2 + 1) * SEQ],
                        scalar=pscale[:, bass.ds(k0 + j, 1)], in1=oT_hi[:, 4 * c + j, :].bitcast(F32),
                        op0=ALU.mult, op1=ALU.subtract)
                ins.then_inc(mT_ready, 1)

            def head(hd, base, first):
                o = 0 if first else NC * RO_U
                for u in range(3 * KD_U + o):
                    if first and u < NC:
                        stream_lo(0, u)
                    split_lo(u, base, 0 if first else RET1 % (2 * RAW))
                    if first and u == 10:
                        row_scale(0)
                    if first and u == 15:
                        dve.wait_ge(p_hi, 1)
                        dve.tensor_tensor(pT_lo[:], p_raw, pT_hi[:].bitcast(F32), ALU.subtract).then_inc(p_split, 1)
                    if not first and u == 2:
                        gate_y(hd - 1)
                    if not first and u == 6:
                        y_lo_part(hd - 1)
                    if u == KD_U + 2:
                        if first:
                            dve.wait_ge(rope_landed, 32)
                        rotate(hd, base + KD_U)
                    for c in range(NC):
                        if not first and u == KD_U + RO_U * (c + 1) + 2:
                            dve.wait_ge(unit_used, base + (KD_U + RO_U * (c + 1)))
                            for t in range(TT):
                                hc = h[:, t, c * COL:(c + 1) * COL]
                                ins = dve.tensor_tensor(hc, acc["BCAB"[c]][t][:], hc, ALU.add)
                            ins.then_inc(o_read, 1)
                    if u == KD_U + o + 4:
                        qkT_lo_part(hd)
                    if u == 2 * KD_U + o:
                        if first:
                            dve.wait_ge(dec_landed, 16)
                        decay_scores(hd)
                    if u == 2 * KD_U + o + 1:
                        pr_lo_part(hd)
                    if u == 2 * KD_U + o + 2:
                        v_lo_part(hd)
                    if u == 2 * KD_U + o + 7:
                        normalise(hd)

            def group(g, base, first, seg):
                o = 0 if first else NC * PO_U
                n2 = g * 2
                for u in range(4 * KD_U + 2 * PO_U + o):
                    split_lo(u, base, seg)
                    if first and u == 2:
                        add_gated(NC - 1)
                    if first and u == 4:
                        stream_lo(2, NC - 1)
                        row_scale(2)
                    if not first and u == 0:
                        m_lo_part(n2 - 2, g * KG - KG, 0)
                    if not first and u == 2:
                        mix(n2 - 1, 1, "B", base)
                    if not first and u == 6:
                        m_lo_part(n2 - 1, g * KG - KG // 2, 1)
                    if u == KD_U + 2:
                        u_lo_part(n2, "A")
                    for c in range(NC):
                        if not first and u == KD_U + PO_U * (c + 1) + 2:
                            dve.wait_ge(unit_used, base + (KD_U + PO_U * (c + 1)))
                            for t in range(TT):
                                hc = h[:, t, c * COL:(c + 1) * COL]
                                ins = dve.tensor_tensor(hc, acc["BCAB"[c]][t][:], hc, ALU.add)
                            ins.then_inc(o_read, 1)
                    if u == (KD_U + 8 if first else KD_U + PO_U + 4):
                        if first:
                            dve.wait_ge(inv_landed, 16)
                        d_scale(g, n2)
                        d_lo_part(n2, 0)
                    if u == 2 * KD_U + o + 2:
                        u_lo_part(n2 + 1, "C")
                    if u == 2 * KD_U + o + 8:
                        d_scale(g, n2 + 1)
                        d_lo_part(n2 + 1, 1)
                    if u == 3 * KD_U + o + 2:
                        gate_p(n2, 0, "A")
                    if u == 4 * KD_U + o + 2:
                        gate_p(n2 + 1, 1, "B")
                    if u == 4 * KD_U + o + PO_U + 2:
                        mix(n2, 0, "C", base + (4 * KD_U + o + PO_U))

            def close(layer, base, ou):
                seg = base % (2 * RAW)
                for u in range(EMB_U + NC * ou + GATE_U):
                    split_lo(u, base, seg)
                    if u == 0 and layer == 1:
                        m_lo_part(2 * GROUPS - 2, (GROUPS - 1) * KG, 0)
                    if u == 2:
                        if layer == 0:
                            gate_y(HEADS - 1)
                        else:
                            mix(2 * GROUPS - 1, 1, "B", base)
                    if u == 5:
                        if layer == 0:
                            y_lo_part(HEADS - 1)
                        else:
                            m_lo_part(2 * GROUPS - 1, (GROUPS - 1) * KG + KG // 2, 1)
                    for c in range(NC):
                        e = EMB_U + ou * (c + 1)
                        if u == e + 2:
                            dve.wait_ge(unit_used, base + e)
                            for t in range(TT):
                                hc = h[:, t, c * COL:(c + 1) * COL]
                                ins = dve.tensor_tensor(hc, acc["BACB"[c]][t][:], hc, ALU.add)
                            ins.then_inc(h_ready, 1)
                        if u == e + 3:
                            stream_lo(2 * layer + 1, c)
                        z = EMB_U + NC * ou + KD_U * (c + 1)
                        if c == 0 and u == z + 1:
                            row_scale(2 * layer + 1)
                        if u == z + 2:
                            add_gated(layer * NC + c)
                            if layer == 1:
                                final_gain_on(c)
                        if u == z + 4 and layer == 0:
                            stream_lo(2, c)

            def final_gain_on(c):
                if c == 0:
                    dve.wait_ge(fgain_landed, 16)
                dve.wait_ge(h_ready, 3 * NC + c + 1)
                dve.tensor_tensor(emb[:, :, c * COL:(c + 1) * COL], h[:, :, c * COL:(c + 1) * COL],
                                  fgain[:, c * COL:(c + 1) * COL].unsqueeze(1).to_broadcast([P, TT, COL]), ALU.mult
                                  ).then_inc(fin_ready, 1)

            dve.wait_ge(gain_landed, 16)
            head(0, RET0, True)
            start = own.n
            own.n = 0
            with dve.Fori(1, HEADS) as hd:
                own.base = hd * HEAD_STEPS + (start - HEAD_STEPS)
                head(hd, hd * HEAD_U + (RET1 - HEAD_U), False)
            assert own.n == HEAD_STEPS, own.n
            own.base, own.n = 0, start + (HEADS - 1) * HEAD_STEPS
            close(0, CLOSE_A, RO_U)
            dve.wait_ge(pscale_landed, 16)
            group(0, POOL0, True, POOL0 % 8)
            with dve.Fori(1, GROUPS) as g:
                group(g, g * GROUP_U + (POOL1 - GROUP_U), False, POOL1 % 8)
            close(1, CLOSE_B, PO_U)
            last = slice(D - COL, D)

            def last_gated(t):
                dve.wait_ge(z_tile, t + 1)
                own.mark(dve.tensor_tensor(sig[:, t, :], sig[:, t, :], emb[:, t, last], ALU.mult))
                own.wait()
                dve.tensor_tensor(h[:, t, last], h[:, t, last], sig[:, t, :], ALU.add).then_inc(h_tile, 1)
                dve.wait_ge(h_tile, t + 1)
                dve.tensor_tensor(emb[:, t, last], h[:, t, last], fgain[:, last], ALU.mult).then_inc(fin_tile, 1)

            def last_row_scale(t):
                dve.wait_ge(ssq_tile, t + 1)
                own.mark(dve.tensor_reduce(rstd[:, t:t + 1], ssq[:, 4, t, :], AX.X, ALU.add))
                own.wait()
                rsqrt(rs[:, 4, t:t + 1], rstd[:, t:t + 1], 1.0 / D, NORM_EPS).then_inc(rs_tile, 1)

            def last_out(t):
                dve.wait_ge(rs_tile, t + 1)
                dve.wait_ge(fin_ready, NC - 1)
                for c in range(NC - ACT_OUT):
                    dve.tensor_scalar(emb[:, t, c * COL:(c + 1) * COL], emb[:, t, c * COL:(c + 1) * COL],
                                      rs[:, 4, t:t + 1], None, ALU.mult).then_inc(out_v, 1)

            last_gated(0)
            last_row_scale(0)
            last_gated(1)
            last_out(0)
            last_row_scale(1)
            last_out(1)


def _tables():
    import numpy as np

    f = np.float32
    pos = np.arange(SEQ, dtype=f)
    freq = f(10000.0) ** (-np.linspace(0.0, 1.0, DK // 2, dtype=f))
    ang = pos[:, None] * freq[None, :]
    cos, sin = np.cos(ang), np.sin(ang)
    cos = np.repeat(cos, 2, axis=1)
    sin = np.stack([-sin, sin], axis=2).reshape(SEQ, DK)
    rope = np.stack([np.tile(a, (1, 2)).reshape(TT, P, 2 * DK).transpose(1, 0, 2) for a in (cos, sin)])

    log_gamma = np.log1p(-(2.0 ** (-5.0 - np.arange(HEADS))))
    diff = np.arange(SEQ)[None, :] - np.arange(P)[:, None]
    decay = np.where(diff[:, None, :] >= 0, np.exp(diff[:, None, :] * log_gamma[None, :, None]), 0.0) * DK ** -0.5

    def block(i0, j0, w):
        i, j = np.arange(i0, i0 + P)[None, :], np.arange(j0, j0 + P)[:, None]
        inside = (i - j >= 0) & (i - j < w)
        return inside.astype(f) - np.where(i == j, np.minimum(i + 1, w), 0).astype(f)

    band = np.stack([np.concatenate([block(0, 0, w), block(P, 0, w), block(P, P, w)], axis=1) for w in WINDOWS], axis=1)
    inv = np.stack([1.0 / np.minimum(np.arange(SEQ) + 1, w) for w in WINDOWS])
    return {
        "rope": rope.astype(f), "decay": decay.astype(f), "band": band.astype(f),
        "counts": np.broadcast_to(inv[None], (P, GROUPS, SEQ)).astype(f), "ident": np.eye(P, dtype=f),
    }


def _stream(ret_in, ret_out, pool_in, pool_group, pool_out, gate_w, proj_w):
    import numpy as np

    stream = np.empty((PIECES * 2, P, UNIT, COL), np.float32)
    n = [0]

    def product(w, k_tiles, k0, *cols):
        for k in range(k0, k0 + k_tiles, UNIT):
            rows = w[k * P:(k + UNIT) * P].reshape(UNIT, P, -1)
            at = 0
            for c, width in cols:
                unit = stream[n[0]]
                unit[:, :, at:at + width] = rows[:, :, c:c + width].transpose(1, 0, 2)
                at += width
            n[0] += 1

    def chunks(w, k_tiles, k0):
        for c in range(NC):
            product(w, k_tiles, k0, (c * COL, COL))

    DV = 2 * DK
    for hd in range(HEADS):
        product(ret_in, KD, 0, (hd * DK, DK), (D + hd * DK, DK))
        if hd:
            chunks(ret_out, 2 * RO_U, (hd - 1) * 2 * RO_U)
        product(ret_in, KD, 0, (2 * D + hd * DV, DV))
        product(ret_in, KD, 0, (4 * D + hd * DV, DV))
    chunks(proj_w[0], KP, 0)
    chunks(ret_out, 2 * RO_U, (HEADS - 1) * 2 * RO_U)
    chunks(gate_w[0], KD, 0)
    for g in range(GROUPS):
        product(pool_in, KD, 0, (g * GDIM, COL))
        if g:
            chunks(pool_out, KG, (g - 1) * KG)
        product(pool_in, KD, 0, (g * GDIM + COL, COL))
        for c in range(2):
            product(pool_in, KD, 0, (2 * D + g * GDIM + c * COL, COL))
        for c in range(2):
            product(pool_group[g], KG, 0, (c * COL, COL))
    chunks(proj_w[1], KP, 0)
    chunks(pool_out, KG, (GROUPS - 1) * KG)
    chunks(gate_w[1], KD, 0)
    assert n[0] == UNITS
    return stream


def kernel(x, p, ret_norm, ret_w_in, ret_w_out, pool_norm, pool_w_in, pool_w_group, pool_scale, pool_w_out,
           ple_norm, ple_w_gate, ple_w_proj, final_norm):
    import numpy as np
    import concourse.bacc as bacc
    from concourse.bass_utils import run_bass_kernel_spmd

    a = {k: np.asarray(v) for k, v in locals().items() if k in (
        "x", "p", "ret_norm", "ret_w_in", "ret_w_out", "pool_norm", "pool_w_in", "pool_w_group", "pool_scale",
        "pool_w_out", "ple_norm", "ple_w_gate", "ple_w_proj", "final_norm")}
    units = _stream(a["ret_w_in"][0], a["ret_w_out"][0], a["pool_w_in"][0], a["pool_w_group"][0],
                    a["pool_w_out"][0], a["ple_w_gate"], a["ple_w_proj"])
    stream = units.reshape(PIECES, 2, P, UNIT * COL).transpose(0, 2, 1, 3).reshape(PIECES, P, PIECE * COL)
    norms = np.stack([a["ret_norm"][0], a["ple_norm"][0], a["pool_norm"][0], a["ple_norm"][1]])
    arrays = {
        "stream": stream,
        "x": a["x"][0],
        "pT": a["p"][:, 0].transpose(0, 2, 1).reshape(2, KP, P, SEQ).transpose(2, 0, 1, 3),
        "gains": norms.reshape(STAGES - 1, KD, P).transpose(2, 0, 1),
        "pool_scale": a["pool_scale"][0].reshape(GROUPS * KG, P).T,
        "final_gain": np.broadcast_to(a["final_norm"][None], (P, D)),
        **_tables(),
    }
    nc = bacc.Bacc("TRN2", target_bir_lowering=False, num_devices=1)
    arrays = {f"in_{k}_dram": np.ascontiguousarray(v) for k, v in arrays.items()}
    args = {k[3:-5]: nc.dram_tensor(k, v.shape, F32, kind="ExternalInput").ap() for k, v in arrays.items()}
    out = nc.dram_tensor("out_dram", (SEQ, D), F32, kind="ExternalOutput").ap()
    trunk(nc, out=out, **args)
    r = run_bass_kernel_spmd(nc, [arrays], core_ids=[0])
    return r.results[0]["out_dram"].reshape(1, SEQ, D)
```
